# Optimizing a Trainium2 kernel written in Bass

```python
import math
import jax, jax.numpy as jnp
from jax import lax
import numpy as np

D_MODEL = 1024
BATCH = 1
SEQ = 256
DEPTH = 2

CHUNK = 64
Q_BLOCK = 128
ROPE_THETA = 500000.0
NORM_EPS = 1e-6
NEG_INF = -1e30

N_EVEN = (DEPTH + 1) // 2
N_ODD = DEPTH // 2

H_A = 8
Q_LORA = 256
KV_LORA = 128
NOPE_A = 64
ROPE_A = 32
V_A = 64
H_B = 8
DH_B = 64
ROT_B = DH_B // 4
H_IDX = 8
D_IDX = 32
ROT_IDX = D_IDX // 4
TOPK_MAX = 256
EVEN_SPLIT_SIZES = (Q_LORA, KV_LORA, ROPE_A, H_B * DH_B, H_B * DH_B, H_B * DH_B, H_IDX * D_IDX, D_IDX, H_IDX)
IN_EVEN = sum(EVEN_SPLIT_SIZES)
MIX_EVEN = H_A * V_A + H_B * DH_B
H_C = 8
DH_C = 64
ROT_C = DH_C // 4
IN_ODD = 3 * H_C * 2 * DH_C
MIX_ODD = H_C * 2 * DH_C
D_FF = 2816
N_EXP = 8
TOP_E = 2
D_FF_E = 3584

kernel_name = 'hybrid_mla_dsa_diffattn_moe_streaming'

def rms_norm(x, g):
    xf = x.astype(jnp.float32)
    y = xf * lax.rsqrt(jnp.mean(jnp.square(xf), axis=-1, keepdims=True) + NORM_EPS)
    return (y * g.astype(jnp.float32)).astype(x.dtype)

def rope_table(seq_len, rot_dim):
    pos = jnp.arange(seq_len, dtype=jnp.float32)
    inv_freq = ROPE_THETA ** (-jnp.arange(0, rot_dim, 2, dtype=jnp.float32) / rot_dim)
    ang = pos[:, None] * inv_freq[None, :]
    return jnp.cos(ang), jnp.sin(ang)

def apply_rope(x, rot_dim):
    S = x.shape[1]
    cos, sin = rope_table(S, rot_dim)
    shp = (1, S) + (1,) * (x.ndim - 3) + (rot_dim // 2,)
    cos = cos.reshape(shp)
    sin = sin.reshape(shp)
    xr = x[..., :rot_dim].astype(jnp.float32)
    x1, x2 = xr[..., :rot_dim // 2], xr[..., rot_dim // 2:]
    rot = jnp.concatenate([x1 * cos - x2 * sin, x2 * cos + x1 * sin], axis=-1).astype(x.dtype)
    return jnp.concatenate([rot, x[..., rot_dim:]], axis=-1)

def chunk_visible(q0, n_keys):
    q_chunk = (q0 + jnp.arange(Q_BLOCK)) // CHUNK
    k_chunk = jnp.arange(n_keys) // CHUNK
    return k_chunk[None, :] <= q_chunk[:, None]

def q_slice(t, q0):
    return lax.dynamic_slice_in_dim(t, q0, Q_BLOCK, axis=1)

def sweep_query_blocks(block_fn, seq_len):
    starts = jnp.arange(seq_len // Q_BLOCK) * Q_BLOCK
    out = lax.map(block_fn, starts)
    out = jnp.moveaxis(out, 0, 1)
    return out.reshape((out.shape[0], seq_len) + out.shape[3:])

def mla_mixer(c_q, c_kv, k_rope, g_q_lat, w_uq, g_kv_lat, w_ukv):
    B, S, _ = c_q.shape
    q = (rms_norm(c_q, g_q_lat) @ w_uq).reshape(B, S, H_A, NOPE_A + ROPE_A)
    q_nope = q[..., :NOPE_A]
    q_pe = apply_rope(q[..., NOPE_A:], ROPE_A)
    kv = (rms_norm(c_kv, g_kv_lat) @ w_ukv).reshape(B, S, H_A, NOPE_A + V_A)
    k_nope, v = kv[..., :NOPE_A], kv[..., NOPE_A:]
    k_pe = apply_rope(k_rope, ROPE_A)
    scale = (NOPE_A + ROPE_A) ** -0.5

    def block(q0):
        qn = q_slice(q_nope, q0)
        qp = q_slice(q_pe, q0)
        s = (jnp.einsum('bqhd,bkhd->bhqk', qn, k_nope, preferred_element_type=jnp.float32)
             + jnp.einsum('bqhr,bkr->bhqk', qp, k_pe, preferred_element_type=jnp.float32)) * scale
        s = jnp.where(chunk_visible(q0, S), s, NEG_INF)
        p = jax.nn.softmax(s, axis=-1).astype(v.dtype)
        return jnp.einsum('bhqk,bkhd->bqhd', p, v)

    return sweep_query_blocks(block, S)

def dsa_mixer(q, k, v, q_idx, k_idx, w_idx, g_idx_k):
    B, S = q.shape[:2]
    top_k = min(TOPK_MAX, S // 4)
    q = apply_rope(q, ROT_B)
    k = apply_rope(k, ROT_B)
    q_idx = apply_rope(q_idx, ROT_IDX)
    k_idx = apply_rope(rms_norm(k_idx, g_idx_k), ROT_IDX)
    w_idx = w_idx.astype(jnp.float32) * (H_IDX ** -0.5)
    idx_scale = D_IDX ** -0.5
    scale = DH_B ** -0.5
    gather = jax.vmap(lambda t, i: t[i])

    def block(q0):
        vis = chunk_visible(q0, S)[None]
        dots = jnp.einsum('bqhd,bkd->bqhk', q_slice(q_idx, q0), k_idx,
                          preferred_element_type=jnp.float32) * idx_scale
        score = jnp.einsum('bqh,bqhk->bqk', q_slice(w_idx, q0), jax.nn.relu(dots))
        score = jnp.where(vis, score, NEG_INF)
        _, sel = lax.top_k(score, top_k)
        sel_ok = jnp.take_along_axis(jnp.broadcast_to(vis, score.shape), sel, axis=-1)
        kg = gather(k, sel)
        vg = gather(v, sel)
        s = jnp.einsum('bqhd,bqkhd->bhqk', q_slice(q, q0), kg, preferred_element_type=jnp.float32) * scale
        s = jnp.where(sel_ok[:, None], s, NEG_INF)
        p = jax.nn.softmax(s, axis=-1).astype(v.dtype)
        return jnp.einsum('bhqk,bqkhd->bqhd', p, vg)

    return sweep_query_blocks(block, S)

def even_mixer(h, w_in, g_q_lat, w_uq, g_kv_lat, w_ukv, g_idx_k, w_out):
    B, S, _ = h.shape
    z = h @ w_in
    splits = np.cumsum(EVEN_SPLIT_SIZES)[:-1].tolist()
    c_q, c_kv, k_rope, q_b, k_b, v_b, q_i, k_i, w_i = jnp.split(z, splits, axis=-1)
    o_a = mla_mixer(c_q, c_kv, k_rope, g_q_lat, w_uq, g_kv_lat, w_ukv)
    o_b = dsa_mixer(q_b.reshape(B, S, H_B, DH_B), k_b.reshape(B, S, H_B, DH_B), v_b.reshape(B, S, H_B, DH_B),
                    q_i.reshape(B, S, H_IDX, D_IDX), k_i, w_i, g_idx_k)
    o = jnp.concatenate([o_a.reshape(B, S, H_A * V_A), o_b.reshape(B, S, H_B * DH_B)], axis=-1)
    return o @ w_out

def diff_mixer(h, w_qkv, lambda_q1, lambda_k1, lambda_q2, lambda_k2, g_sub, w_out, layer):
    B, S, _ = h.shape
    lambda_init = 0.8 - 0.6 * math.exp(-0.3 * layer)
    q, k, v = jnp.split(h @ w_qkv, 3, axis=-1)
    q = apply_rope(q.reshape(B, S, H_C, 2, DH_C), ROT_C)
    k = apply_rope(k.reshape(B, S, H_C, 2, DH_C), ROT_C)
    v = v.reshape(B, S, H_C, 2 * DH_C)
    f32 = jnp.float32
    lam = (jnp.exp(jnp.sum(lambda_q1.astype(f32) * lambda_k1.astype(f32)))
           - jnp.exp(jnp.sum(lambda_q2.astype(f32) * lambda_k2.astype(f32))) + lambda_init)
    scale = DH_C ** -0.5

    def block(q0):
        s = jnp.einsum('bqhcd,bkhcd->bhcqk', q_slice(q, q0), k, preferred_element_type=jnp.float32) * scale
        s = jnp.where(chunk_visible(q0, S), s, NEG_INF)
        p = jax.nn.softmax(s, axis=-1)
        a = (p[:, :, 0] - lam * p[:, :, 1]).astype(v.dtype)
        return jnp.einsum('bhqk,bkhd->bqhd', a, v)

    o = sweep_query_blocks(block, S)
    o = rms_norm(o, g_sub) * (1.0 - lambda_init)
    return o.reshape(B, S, MIX_ODD) @ w_out

def swiglu(h, w_gate, w_up, w_down):
    return (jax.nn.silu(h @ w_gate) * (h @ w_up)) @ w_down

def moe_ffn(h, w_router, w_gate, w_up, w_down):
    logits = (h @ w_router).astype(jnp.float32)
    top_logit, top_idx = lax.top_k(logits, TOP_E)
    gates = jax.nn.softmax(top_logit, axis=-1)
    combine = jnp.sum(jax.nn.one_hot(top_idx, N_EXP, dtype=jnp.float32) * gates[..., None], axis=-2)
    out = jnp.zeros_like(h)
    for e in range(N_EXP):
        out = out + combine[..., e:e + 1].astype(h.dtype) * swiglu(h, w_gate[e], w_up[e], w_down[e])
    return out

def setup_inputs(seed: int = 0) -> dict:
    key = jax.random.key(seed)
    keys = jax.random.split(key, 32)
    kl = [keys[i] for i in range(32)]
    f32 = jnp.float32

    def w(i, shape, fan_in):
        return jax.random.normal(kl[i], shape, f32) * fan_in ** -0.5

    def gain(i, shape):
        return 1.0 + 0.02 * jax.random.normal(kl[i], shape, f32)

    E, O = N_EVEN, N_ODD
    return {
        'x': jax.random.normal(kl[0], (BATCH, SEQ, D_MODEL), f32),
        'ev_norm_mix': gain(1, (E, D_MODEL)),
        'ev_w_in': w(2, (E, D_MODEL, IN_EVEN), D_MODEL),
        'ev_g_q_lat': gain(3, (E, Q_LORA)),
        'ev_w_uq': w(4, (E, Q_LORA, H_A * (NOPE_A + ROPE_A)), Q_LORA),
        'ev_g_kv_lat': gain(5, (E, KV_LORA)),
        'ev_w_ukv': w(6, (E, KV_LORA, H_A * (NOPE_A + V_A)), KV_LORA),
        'ev_g_idx_k': gain(7, (E, D_IDX)),
        'ev_w_out': w(8, (E, MIX_EVEN, D_MODEL), MIX_EVEN),
        'ev_norm_ffn': gain(9, (E, D_MODEL)),
        'ev_w_gate': w(10, (E, D_MODEL, D_FF), D_MODEL),
        'ev_w_up': w(11, (E, D_MODEL, D_FF), D_MODEL),
        'ev_w_down': w(12, (E, D_FF, D_MODEL), D_FF),
        'od_norm_mix': gain(13, (O, D_MODEL)),
        'od_w_qkv': w(14, (O, D_MODEL, IN_ODD), D_MODEL),
        'od_lambda_q1': 0.1 * jax.random.normal(kl[15], (O, DH_C), f32),
        'od_lambda_k1': 0.1 * jax.random.normal(kl[16], (O, DH_C), f32),
        'od_lambda_q2': 0.1 * jax.random.normal(kl[17], (O, DH_C), f32),
        'od_lambda_k2': 0.1 * jax.random.normal(kl[18], (O, DH_C), f32),
        'od_g_sub': gain(19, (O, 2 * DH_C)),
        'od_w_out': w(20, (O, MIX_ODD, D_MODEL), MIX_ODD),
        'od_norm_ffn': gain(21, (O, D_MODEL)),
        'od_w_router': w(22, (O, D_MODEL, N_EXP), D_MODEL),
        'od_w_gate_e': w(23, (O, N_EXP, D_MODEL, D_FF_E), D_MODEL),
        'od_w_up_e': w(24, (O, N_EXP, D_MODEL, D_FF_E), D_MODEL),
        'od_w_down_e': w(25, (O, N_EXP, D_FF_E, D_MODEL), D_FF_E),
        'final_norm': gain(26, (D_MODEL,)),
    }

def reference(x, ev_norm_mix, ev_w_in, ev_g_q_lat, ev_w_uq, ev_g_kv_lat, ev_w_ukv, ev_g_idx_k, ev_w_out,
              ev_norm_ffn, ev_w_gate, ev_w_up, ev_w_down,
              od_norm_mix, od_w_qkv, od_lambda_q1, od_lambda_k1, od_lambda_q2, od_lambda_k2, od_g_sub, od_w_out,
              od_norm_ffn, od_w_router, od_w_gate_e, od_w_up_e, od_w_down_e,
              final_norm):
    h = x
    for layer in range(DEPTH):
        i = layer // 2
        if layer % 2 == 0:
            h = h + even_mixer(rms_norm(h, ev_norm_mix[i]), ev_w_in[i], ev_g_q_lat[i], ev_w_uq[i],
                               ev_g_kv_lat[i], ev_w_ukv[i], ev_g_idx_k[i], ev_w_out[i])
            h = h + swiglu(rms_norm(h, ev_norm_ffn[i]), ev_w_gate[i], ev_w_up[i], ev_w_down[i])
        else:
            h = h + diff_mixer(rms_norm(h, od_norm_mix[i]), od_w_qkv[i], od_lambda_q1[i], od_lambda_k1[i],
                               od_lambda_q2[i], od_lambda_k2[i], od_g_sub[i], od_w_out[i], layer)
            h = h + moe_ffn(rms_norm(h, od_norm_ffn[i]), od_w_router[i], od_w_gate_e[i], od_w_up_e[i],
                            od_w_down_e[i])
    return rms_norm(h, final_norm)


_drawn_inputs = setup_inputs


def setup_inputs(seed=0):
    import zlib

    import numpy as np

    out = dict(_drawn_inputs(seed))
    spreads = {}
    factors = {'ev_g_q_lat': 3.838,
     'od_norm_mix': 2.691,
     'final_norm': 22.131,
     'od_lambda_k1': 3.233,
     'od_lambda_k2': 5.143,
     'od_g_sub': 3.308,
     'od_norm_ffn': 3.071}
    for name, (base, spread) in spreads.items():
        noise = np.random.default_rng([zlib.crc32(name.encode()), seed]).standard_normal(out[name].shape)
        drawn = base * np.exp(spread * noise) if base else spread * noise
        out[name] = __import__('jax').numpy.asarray(drawn.astype(out[name].dtype))
    for name, factor in factors.items():
        out[name] = (out[name] * factor).astype(out[name].dtype)
    return out
```

```python
import math
from contextlib import ExitStack

import concourse.bass as bass
from concourse import mybir

ALU = mybir.AluOpType
ACT = mybir.ActivationFunctionType
AX = mybir.AxisListType
F32 = mybir.dt.float32
F32R = mybir.dt.float32r
I32 = mybir.dt.int32
U32 = mybir.dt.uint32

P = 128
S, D = 256, 1024
T = S // P
KC = D // P
EPS = 1e-6
NEG = -1e30
TAKEN = -3e38
TOP_K = 64
H = 8
NOPE, ROPE_A, V_A = 64, 32, 64
DH = 64
Q_LORA, KV_LORA = 256, 128
D_IDX = 32
D_FF, D_FF_E, N_EXP = 2816, 3584, 8
IN_EVEN = 2248
C_Q, C_KV, K_ROPE, Q_B, K_B, V_B, Q_I, K_I, W_I = 0, 256, 384, 416, 928, 1440, 1952, 2208, 2240
K_REP = 2304
V_MLA = 2560
ZW = 3072
LAMBDA_INIT = 0.8 - 0.6 * math.exp(-0.3)

RAW, HL = 7, 3
TW = 2048
T_IN, T_UQ, T_UKV, T_OUT0 = 0, 10, 11, 12
T_FFN = 16
FFN_STEPS = 6
T_QKV = T_FFN + 33
T_OUT1 = T_QKV + 12
T_MOE = T_OUT1 + 4
AHEAD = 3
E_STEPS = D_FF_E // 512
JOB = 6 * E_STEPS
MAX_OVER = 3
COLS = N_EXP + MAX_OVER + 1
assert JOB % RAW == 0 and JOB % HL == 0

HEAD_MS, LAM, NEG_LAM = 64, 80, 84
G_MIX0, G_QL, G_KV, G_FFN0, G_MIX1, G_SUB, G_FFN1, N_GAINS = 0, 8, 10, 11, 19, 27, 28, 36
K_ID, K_IOTA, K_TRI, K_HID, K_E, N_CONST = 0, 128, 256, 384, 768, 776
R_16, R_8, R_4, N_ROT = 0, 32, 48, 56


def ffn_tiles(n):
    if n == 0:
        return [0, 1], [2, 3], []
    if n < FFN_STEPS - 1:
        b = 4 + 6 * (n - 1)
        return [b, b + 1], [b + 2, b + 3], [b + 4, b + 5]
    if n == FFN_STEPS - 1:
        return [28], [29], [30, 31]
    return [], [], [32]


def job_tiles(n):
    if n == 0:
        return [0, 1], [2, 3], []
    b = 4 + 6 * (n - 1)
    if n < E_STEPS:
        return [b, b + 1], [b + 2, b + 3], [b + 4, b + 5]
    return [], [], [b, b + 1]


def trunk(nc, a):
    x_in, consts_in, rope_in, out = a["x"], a["consts"], a["rope"], a["out"]
    with ExitStack() as ctx:
        base = 16512
        limit = 229368

        def at(name, offset, shape, dt=F32):
            return nc.alloc_sbuf_tensor_at(name, shape, dt, offset=offset).ap()

        top = [base]

        def sb(name, shape, dt=F32):
            size = 4
            for n in shape[1:]:
                size *= n
            o = top[0]
            top[0] = (o + size + 31) // 32 * 32
            assert top[0] <= limit, (name, top[0])
            return at(name, o, shape, dt), o

        def sem(name):
            return ctx.enter_context(nc.semaphore(name))

        raw, _ = sb("raw", [P, RAW, TW])
        w_hi, _ = sb("w_hi", [P, HL, TW], F32R)
        w_lo, _ = sb("w_lo", [P, HL, TW], F32R)
        x, _ = sb("x_sb", [P, T, D])
        xt_hi, _ = sb("xt_hi", [P, KC, S], F32R)
        xt_lo, _ = sb("xt_lo", [P, KC, S], F32R)
        z, z_at = sb("z", [P, T, ZW])
        qa, qa_at = sb("qa", [P, T, H, NOPE + ROPE_A])
        ka, ka_at = sb("ka", [P, T, H, NOPE + ROPE_A])
        qk_t, qk_at = sb("qk_t", [P, 2, KC, S])
        idx_t, _ = sb("idx_t", [P, 3, S])
        sc, sc_at = sb("sc", [P, 3, 512])
        pr, pr_at = sb("pr", [P, 3, 512])
        pt, _ = sb("pt", [P, 2, 2, P])
        cst, _ = sb("cst", [P, N_CONST])
        rope, _ = sb("rope_sb", [P, T, N_ROT])
        key_mask, _ = sb("key_mask", [P, T, S])
        gains, _ = sb("gains", [P, N_GAINS])
        stat, _ = sb("stat", [P, 96])
        sums, _ = sb("sums", [P, 64])
        peak, _ = sb("peak", [P, 4, 2])
        recip, _ = sb("recip", [P, 8])
        top8, _ = sb("top8", [P, 8])
        over, _ = sb("over", [P, 5], I32)
        xn = at("xn", z_at + 16384, [P, T, D])
        sg = at("sg", z_at, [P, T, 512])
        hh = at("hh", z_at + 4096, [P, T, 512])
        ht_hi = at("ht_hi", z_at + 8192, [P, 4, S], F32R)
        ht_lo = at("ht_lo", z_at + 12288, [P, 4, S], F32R)
        o_a = at("o_a", qa_at, [P, T, 512])
        xn_hi = at("xn_hi", qk_at, [P, T, D], F32R)
        xn_lo = at("xn_lo", qk_at + 8192, [P, T, D], F32R)
        xg_hi = at("xg_hi", z_at + 16384, [P, KC, P], F32R)
        xg_lo = at("xg_lo", z_at + 20480, [P, KC, P], F32R)
        y_hi = at("y_hi", qa_at, [P, D], F32R)
        y_lo = at("y_lo", qa_at + 4096, [P, D], F32R)
        sel = at("sel", qa_at + 8192, [P, T, P], F32R)
        sel_t = at("sel_t", qa_at + 9216, [P, S], F32R)
        ident_r = at("ident_r", qa_at + 10240, [P, P], F32R)
        place = at("place", qa_at + 10752, [P, T, COLS])
        gate = at("gate", qa_at + 10752 + 96, [P, T, COLS])
        place_now = at("place_now", qa_at + 10944, [P, T])
        gate_now = at("gate_now", qa_at + 10976, [P, T])
        moe_s = at("moe_s", pr_at + 4928, [P, 240])
        top_i = at("top_i", pr_at + 4864, [P, T, 8], U32)
        logit_rows = at("logit_rows", sc_at, [N_EXP, S])
        over_s = at("over_s", sc_at + 1024, [P, 144])
        wr = at("wr", pr_at + 4096, [P, KC, N_EXP])
        wr_hi = at("wr_hi", pr_at + 4352, [P, KC, N_EXP], F32R)
        wr_lo = at("wr_lo", pr_at + 4608, [P, KC, N_EXP], F32R)
        final_gain = at("final_gain", pr_at, [P, D])
        g_idx = at("g_idx", pr_at + 4096, [P, D_IDX])
        lam_in = at("lam_in", pr_at + 4096 + 128, [P, 4, DH])
        gain_rows = at("gain_rows", pr_at, [N_GAINS, P])
        junk = at("junk", sc_at, [P, D])

        ident = cst[:, K_ID:K_ID + P]
        iota = cst[:, K_IOTA:K_IOTA + P]
        tri = cst[:, K_TRI:K_TRI + P]
        iota_e = cst[:, K_E:K_E + 8]
        ones, _ = sb("ones", [P, P])
        hidden = [cst[:, K_HID:K_HID + P], cst[:, K_HID + P:K_HID + P + S]]

        B = [nc.alloc_psum_tensor(f"bank{i}", [P, 512], F32).ap() for i in range(8)]

        x_landed = sem("x_landed")
        cst_landed = sem("cst_landed")
        mix_landed = sem("mix_landed")
        small_landed = sem("small_landed")
        raw_landed = [sem(f"raw_landed{i}") for i in range(RAW)]
        hi_ready = sem("hi_ready")
        lo_ready = sem("lo_ready")
        tile_used = sem("tile_used")
        ones_set = sem("ones_set")
        gains_t = sem("gains_t")
        gains_ready = sem("gains_ready")
        squares = sem("squares")
        var_ready = sem("var_ready")
        root_ready = sem("root_ready")
        src_ready = sem("src_ready")
        fill_t = sem("fill_t")
        fill_hi = sem("fill_hi")
        fill_lo = sem("fill_lo")
        unit_out = [sem(f"unit_out{q}") for q in range(19)]
        v_step = sem("v_step")
        s_step = sem("s_step")
        turn_t = sem("turn_t")
        turn_s = sem("turn_s")
        turn_v = sem("turn_v")
        rot_ready = sem("rot_ready")
        ix_dots = sem("ix_dots")
        ix_relu = sem("ix_relu")
        ix_sum = sem("ix_sum")
        scores = sem("scores")
        masked = sem("masked")
        exps = sem("exps")
        mixed = sem("mixed")
        probs_t = sem("probs_t")
        probs_out = sem("probs_out")
        pv = sem("pv")
        o_out = sem("o_out")
        lam_dots = sem("lam_dots")
        lam_exp = sem("lam_exp")
        f_silu = sem("f_silu")
        f_h = sem("f_h")
        f_t = sem("f_t")
        f_thi = sem("f_thi")
        f_tlo = sem("f_tlo")
        f_add = sem("f_add")
        xn_split = sem("xn_split")
        xn_split_lo = sem("xn_split_lo")
        wr_split = sem("wr_split")
        wr_split_lo = sem("wr_split_lo")
        logits_t = sem("logits_t")
        logits_out = sem("logits_out")
        logits = sem("logits")
        chosen = sem("chosen")
        gate_exp = sem("gate_exp")
        places = sem("places")
        place_copied = sem("place_copied")
        routed = sem("routed")
        m_silu = sem("m_silu")
        m_h = sem("m_h")
        m_t = sem("m_t")
        m_thi = sem("m_thi")
        m_tlo = sem("m_tlo")
        sel_ready = sem("sel_ready")
        gathered = sem("gathered")
        xg_hi_ready = sem("xg_hi_ready")
        xg_lo_ready = sem("xg_lo_ready")
        sel_turned = sem("sel_turned")
        sel_t_ready = sem("sel_t_ready")
        y_hi_ready = sem("y_hi_ready")
        y_lo_ready = sem("y_lo_ready")
        scattered = sem("scattered")
        added = sem("added")
        late_landed = sem("late_landed")
        done = sem("done")
        stored = sem("stored")

        def col_tile(w, half, c0, width):
            return w.rearrange("(c p) f -> p c f", p=P)[:, 4 * half:4 * half + 4, c0:c0 + width]

        w_in, w_out0, w_qkv, w_out1 = a["ev_w_in"][0], a["ev_w_out"][0], a["od_w_qkv"][0], a["od_w_out"][0]
        fg, fu, fd = a["ev_w_gate"][0], a["ev_w_up"][0], a["ev_w_down"][0]

        def slot(tile3, i, chunks, width):
            return tile3[:, i, 0:chunks * width].rearrange("p (c f) -> p c f", c=chunks)

        def pre_tiles():
            t = []
            for q in range(5):
                width = min(512, IN_EVEN - 512 * q)
                t += [(4, width, col_tile(w_in, hf, 512 * q, width)) for hf in range(2)]
            t.append((2, 768, a["ev_w_uq"][0].rearrange("(c p) f -> p c f", p=P)))
            t.append((1, 1024, a["ev_w_ukv"][0].rearrange("(c p) f -> p c f", p=P)))
            t += [(4, 512, col_tile(w_out0, hf, 512 * q, 512)) for q in range(2) for hf in range(2)]

            def down(n):
                return [(4, 512, fd.rearrange("(c p) f -> p c f", p=P)[:, 4 * n:4 * n + 4, 512 * hf:512 * hf + 512])
                        for hf in range(2)]
            for n in range(FFN_STEPS - 1):
                for w in (fg, fu):
                    t += [(4, 512, col_tile(w, hf, 512 * n, 512)) for hf in range(2)]
                if n:
                    t += down(n - 1)
            for w in (fg, fu):
                t.append((8, 256, w.rearrange("(c p) f -> p c f", p=P)[:, :, 2560:2816]))
            t += down(FFN_STEPS - 2)
            t.append((2, 1024, fd.rearrange("(c p) f -> p c f", p=P)[:, 20:22, :]))
            t += [(4, 512, col_tile(w_qkv, hf, 512 * q, 512)) for q in range(6) for hf in range(2)]
            t += [(4, 512, col_tile(w_out1, hf, 512 * q, 512)) for q in range(2) for hf in range(2)]
            assert len(t) == T_MOE
            return t

        PRE = pre_tiles()
        size_of = [c * w for c, w, _ in PRE]

        def turn_idx(g):
            return (idx_t[:, 0:2, :].rearrange("p c t -> p (c t)"), P, 512) if g == 0 else (idx_t[:, 2, :], P, S)

        def turn_a(g):
            return qk_t[0:NOPE + ROPE_A, g // 4, 2 * (g % 4):2 * (g % 4) + 2, :].rearrange("p c t -> p (c t)"), NOPE + ROPE_A, 512

        def turn_b(g):
            return qk_t[:, g // 2, 2 * (g % 2):2 * (g % 2) + 2, :].rearrange("p c t -> p (c t)"), P, 512

        def turn_c(g):
            return qk_t[:, g // 4, 2 * (g % 4):2 * (g % 4) + 2, :].rearrange("p c t -> p (c t)"), P, 512

        block = ctx.enter_context(nc.Block())

        @block.sync
        def _(sp):
            sp.dma_start(x[:, :, :], x_in[0].rearrange("(b p) d -> p b d", p=P)).then_inc(x_landed, 16)
            for i, (chunks, width, src) in enumerate(PRE):
                if i >= RAW:
                    sp.wait_ge(lo_ready, i - RAW + 1)
                sp.dma_start(slot(raw, i % RAW, chunks, width), src).then_inc(raw_landed[i % RAW], 16)

            def load(j, e, wanted):
                gate_w = a["od_w_gate_e"][0, bass.ds(e, 1)].rearrange("o (c p) f -> p (o c) f", p=P)
                up_w = a["od_w_up_e"][0, bass.ds(e, 1)].rearrange("o (c p) f -> p (o c) f", p=P)
                down_w = a["od_w_down_e"][0, bass.ds(e, 1)].rearrange("o (c p) f -> p (o c) f", p=P)
                for n in range(E_STEPS + 1):
                    g, u, d = job_tiles(n)
                    srcs = [gate_w[:, 4 * k:4 * k + 4, 512 * n:512 * n + 512] for k in range(len(g))]
                    srcs += [up_w[:, 4 * k:4 * k + 4, 512 * n:512 * n + 512] for k in range(len(u))]
                    srcs += [down_w[:, 4 * n - 4:4 * n, 512 * k:512 * k + 512] for k in range(len(d))]
                    for i, src in zip(g + u + d, srcs):
                        if i in wanted:
                            s = (T_MOE + i) % RAW
                            sp.wait_ge(lo_ready, j * JOB + T_MOE + i - RAW + 1)
                            sp.dma_start(slot(raw, s, 4, 512), src).then_inc(raw_landed[s], 16)

            head, rest = range(2), range(2, JOB)
            load(0, 0, head)
            with sp.Fori(0, N_EXP - 1) as j:
                load(j, j, rest)
                load(j + 1, j + 1, head)
            load(N_EXP - 1, N_EXP - 1, rest)
            sp.wait_ge(routed, 1)
            n_over = sp.value_load(over[0:1, 0:1], min_val=0, max_val=MAX_OVER)
            load(N_EXP, sp.value_load(over[0:1, 1:2], min_val=0, max_val=N_EXP - 1), head)
            with sp.If(n_over > 0):
                with sp.Fori(0, n_over) as i:
                    load(i + N_EXP, sp.value_load(over[0:1, bass.ds(i + 1, 1)], min_val=0, max_val=N_EXP - 1), rest)
                    load(i + (N_EXP + 1), sp.value_load(over[0:1, bass.ds(i + 2, 1)], min_val=0, max_val=N_EXP - 1), head)
            load(n_over + N_EXP, 0, range(2, AHEAD))
            for b in range(T):
                sp.wait_ge(done, b + 1)
                sp.dma_start(out[0].rearrange("(b p) d -> b p d", p=P)[b], x[:, b]).then_inc(stored, 16)
            sp.wait_ge(stored, 16 * T)

        @block.scalar
        def _(act):
            act.dma_start(cst[:, :], consts_in).then_inc(cst_landed, 16)
            act.dma_start(gain_rows[G_MIX0:G_MIX0 + 8, :], a["ev_norm_mix"][0].rearrange("(c p) -> c p", p=P)).then_inc(mix_landed, 16)

            def hi_part(i, size=None):
                size = size_of[i] if size is None else size
                act.wait_ge(raw_landed[i % RAW], 16 * (i // RAW + 1))
                if i >= HL:
                    act.wait_ge(tile_used, i - HL + 1)
                act.activation(w_hi[:, i % HL, 0:size], raw[:, i % RAW, 0:size], ACT.Copy).then_inc(hi_ready, 1)

            def job_hi(j, i):
                g = T_MOE + i
                act.wait_ge(raw_landed[g % RAW], j * (16 * JOB // RAW) + 16 * (g // RAW + 1))
                act.wait_ge(tile_used, j * JOB + g - HL + 1)
                act.activation(w_hi[:, g % HL, :], raw[:, g % RAW, :], ACT.Copy).then_inc(hi_ready, 1)

            counts = {"squares": 0, "var": 0}

            def token_squares(col):
                for b in range(T):
                    if b:
                        act.wait_ge(squares, counts["squares"])
                    act.activation(junk, x[:, b], ACT.Square, scale=1.0 / 32, accum_out=stat[:, col + b:col + b + 1])\
                       .then_inc(squares, 1)
                    counts["squares"] += 1

            def root(c0, n):
                counts["var"] += 1
                act.wait_ge(var_ready, counts["var"])
                act.activation(stat[:, c0:c0 + n], stat[:, c0:c0 + n], ACT.Sqrt).then_inc(root_ready, 1)

            filled = [0, 0]

            def fill(gain, banks=4, per=2):
                for g in range(banks):
                    filled[1] += 1
                    act.wait_ge(fill_t, filled[1])
                    for c in range(per * g, min(per * g + per, per * banks)):
                        if gain is None:
                            scale = 1.0
                        else:
                            if gain(c) is None:
                                continue
                            scale = gains[:, gain(c):gain(c) + 1]
                        act.activation(xt_hi[:, c, :], B[4 + g][:, (c % per) * S:(c % per + 1) * S], ACT.Copy, scale=scale)\
                           .then_inc(fill_hi, 1)
                        filled[0] += 1

            def unit(q, tile, out_ap):
                act.wait_ge(tile_used, tile + 1)
                act.activation(out_ap, B[2 * (q % 2)][:, 0:out_ap.shape[-1]], ACT.Copy).then_inc(unit_out[q], 1)

            act.wait_ge(x_landed, 16)
            token_squares(0)
            root(0, 2)
            hi_part(0)
            act.wait_ge(gains_ready, 1)
            fill(lambda c: G_MIX0 + c)
            for i in range(1, HL):
                hi_part(i)
            for q in range(5):
                for i in (2 * q, 2 * q + 1):
                    if i >= HL:
                        hi_part(i)
                if q:
                    unit(q - 1, 2 * q - 1, z[:, 0, 512 * (q - 1):512 * q])
            hi_part(T_UQ)
            unit(4, T_IN + 9, z[:, 0, 2048:IN_EVEN])
            hi_part(T_UKV)
            hi_part(T_OUT0)
            act.wait_ge(unit_out[0], 2)
            act.wait_ge(unit_out[4], 2)
            for k, (c0, n) in enumerate(((C_Q, Q_LORA), (C_KV, KV_LORA), (K_I, D_IDX))):
                for b in range(T):
                    act.wait_ge(squares, counts["squares"])
                    act.activation(junk[:, 0:n], z[:, b, c0:c0 + n], ACT.Square, scale=n ** -0.5,
                                   accum_out=stat[:, 8 + 2 * k + b:9 + 2 * k + b]).then_inc(squares, 1)
                    counts["squares"] += 1
            root(8, 6)
            act.wait_ge(gains_ready, 2)
            fill(lambda c: (G_QL + c if c < 3 else None), banks=2)
            act.wait_ge(tile_used, T_UQ + 1)
            act.activation(qa[:, 0].rearrange("p h d -> p (h d)")[:, 0:512], B[2][:, 0:512], ACT.Copy).then_inc(unit_out[5], 1)
            act.activation(qa[:, 0].rearrange("p h d -> p (h d)")[:, 512:768], B[0][:, 0:256], ACT.Copy).then_inc(unit_out[6], 1)
            act.wait_ge(tile_used, T_UKV + 1)
            for q in range(2):
                src = B[4 if q == 0 else 6].rearrange("p (h d) -> p h d", h=4)
                act.activation(ka[:, 0, 4 * q:4 * q + 4, 0:NOPE], src[:, :, 0:NOPE], ACT.Copy).then_inc(unit_out[7 + q], 1)
                act.activation(z[:, 0, V_MLA + 256 * q:V_MLA + 256 * q + 256].rearrange("p (h d) -> p h d", h=4),
                               src[:, :, NOPE:], ACT.Copy).then_inc(unit_out[7 + q], 1)

            def turn(first, n, dst):
                for g in range(n):
                    if (first + g) % 2 == 0:
                        act.wait_ge(turn_t, first + g + 1)
                        d, parts, width = dst(g)
                        act.activation(d, B[(first + g) % 4][0:parts, 0:width], ACT.Copy).then_inc(turn_s, 1)

            turn(0, 2, turn_idx)
            turn(2, 8, turn_a)
            for u in range(2 * H):
                act.wait_ge(ix_dots, u + 1)
                if u >= 3:
                    act.wait_ge(ix_sum, u - 2)
                nk = P * (u // H + 1)
                act.activation(sc[:, u % 3, 0:nk], B[u % 3][:, 0:nk], ACT.Relu, scale=(H * D_IDX) ** -0.5)\
                   .then_inc(ix_relu, 1)

            def attend(u0, maps):
                for i in range(2 * H + 2):
                    u = u0 + i
                    if i < 2 * H:
                        nk = P * (i // H + 1)
                        act.wait_ge(masked, u + 1)
                        if u >= 3:
                            act.wait_ge(probs_t, u - 2)
                        for c in range(maps):
                            k = 2 * H * (u0 // (2 * H)) + i * maps + c
                            e = act.activation(pr[:, u % 3, c * S:c * S + nk], sc[:, u % 3, c * S:c * S + nk], ACT.Exp,
                                               bias=peak[:, u % 3, c:c + 1], scale=-1.0,
                                               accum_out=sums[:, k:k + 1])
                        e.then_inc(exps, 1)
                    if i >= 2:
                        v = u - 2
                        nk = P * ((i - 2) // H + 1)
                        act.wait_ge(probs_t, v + 1)
                        if v >= 2:
                            act.wait_ge(pv, v - 1)
                        act.activation(pt[:, v % 2].rearrange("p k q -> p (k q)")[:, 0:nk], B[3 + v % 2][:, 0:nk], ACT.Copy)\
                           .then_inc(probs_out, 1)

            act.wait_ge(lam_dots, 2)
            act.activation(stat[:, LAM:LAM + 2], stat[:, LAM:LAM + 2], ACT.Exp).then_inc(lam_exp, 1)
            attend(0, 1)
            turn(10, 4, turn_b)
            attend(2 * H, 1)
            for i in (T_OUT0 + 1, T_OUT0 + 2):
                hi_part(i)
            fill(None)
            hi_part(T_OUT0 + 3)

            hi_part(T_FFN)
            hi_part(T_FFN + 1)
            act.wait_ge(unit_out[10], 2)
            act.wait_ge(unit_out[9], 2)
            token_squares(2)
            root(2, 2)
            fill(lambda c: G_FFN0 + c)
            hi_part(T_FFN + 2)
            for n in range(FFN_STEPS + 1):
                g, u, d = ffn_tiles(n)
                w = 512 if n < FFN_STEPS - 1 else 256
                for i in g + u:
                    if i > 2:
                        hi_part(T_FFN + i)
                if g:
                    act.wait_ge(tile_used, T_FFN + g[-1] + 1)
                    for b in range(T):
                        if n:
                            act.wait_ge(f_h, 2 * n)
                        act.activation(sg[:, b, 0:w], B[b][:, 0:w], ACT.Silu).then_inc(f_silu, 1)
                if n == FFN_STEPS:
                    for i in d:
                        hi_part(T_FFN + i)
                if d:
                    c = 4 if n < FFN_STEPS else 2
                    for b in range(T):
                        act.wait_ge(f_t, 2 * (n - 1) + b + 1)
                        act.activation(ht_hi[:, 0:c, b * P:b * P + P], B[4][:, 0:c * P].rearrange("p (c t) -> p c t", c=c),
                                       ACT.Copy).then_inc(f_thi, 1)
                    if n < FFN_STEPS:
                        for i in d:
                            hi_part(T_FFN + i)

            hi_part(T_QKV)
            hi_part(T_QKV + 1)
            act.wait_ge(f_add, 4 * FFN_STEPS)
            token_squares(4)
            root(4, 2)
            fill(lambda c: G_MIX1 + c)
            hi_part(T_QKV + 2)
            for q in range(6):
                for i in (2 * q, 2 * q + 1):
                    if i >= HL:
                        hi_part(T_QKV + i)
                if q:
                    unit(11 + q - 1, T_QKV + 2 * q - 1, z[:, 0, 512 * (q - 1):512 * q])
            hi_part(T_OUT1)
            unit(16, T_QKV + 11, z[:, 0, 2560:3072])
            turn(14, 8, turn_c)
            attend(4 * H, 2)
            root(64, 16)
            for i in (T_OUT1 + 1, T_OUT1 + 2):
                hi_part(i)
            fill(lambda c: G_SUB)
            hi_part(T_OUT1 + 3)

            act.wait_ge(late_landed, 32)
            act.activation(wr_hi[:, :, :], wr[:, :, :], ACT.Copy).then_inc(wr_split, 1)
            act.wait_ge(unit_out[17], 2)
            act.wait_ge(unit_out[18], 2)
            token_squares(6)
            root(6, 2)
            fill(lambda c: G_FFN1 + c)
            for b in range(T):
                act.activation(xn_hi[:, b], xn[:, b], ACT.Copy).then_inc(xn_split, 1)
            act.activation(ident_r, ident, ACT.Copy).then_inc(wr_split, 1)
            for i in range(AHEAD):
                job_hi(0, i)
            act.wait_ge(chosen, 1)
            act.activation(moe_s[:, 32:34], moe_s[:, 32:34], ACT.Exp).then_inc(gate_exp, 1)

            def take_gathered(j):
                for k in range(2):
                    act.wait_ge(gathered, j * 2 + k + 1)
                    for c in range(4 * k, 4 * k + 4):
                        e = act.activation(xg_hi[:, c, :], B[1 + 2 * k][:, (c % 4) * P:(c % 4 + 1) * P], ACT.Copy,
                                           scale=gains[:, G_FFN1 + c:G_FFN1 + c + 1])
                    e.then_inc(xg_hi_ready, 1)

            def take_turned(j):
                act.wait_ge(sel_turned, j + 1)
                act.activation(sel_t[:, :], B[7][:, 0:S], ACT.Copy).then_inc(sel_t_ready, 1)

            take_gathered(0)
            take_turned(0)

            def job(j):
                for n in range(E_STEPS + 1):
                    g, u, d = job_tiles(n)
                    for i in g + u:
                        if i >= AHEAD:
                            job_hi(j, i)
                    if g:
                        act.wait_ge(tile_used, j * JOB + T_MOE + g[-1] + 1)
                        if n:
                            act.wait_ge(m_h, j * E_STEPS + n)
                        act.activation(sg[:, 0], B[0][:, :], ACT.Silu).then_inc(m_silu, 1)
                    if n == E_STEPS:
                        for i in d:
                            job_hi(j, i)
                    if d:
                        act.wait_ge(m_t, j * E_STEPS + n)
                        act.activation(ht_hi[:, :, 0:P], B[4].rearrange("p (c t) -> p c t", c=4), ACT.Copy)\
                           .then_inc(m_thi, 1)
                    if d and n < E_STEPS:
                        for i in d:
                            job_hi(j, i)
                take_gathered(j + 1)
                for i in range(AHEAD):
                    if i:
                        act.wait_ge(tile_used, j * JOB + T_MOE + JOB - 2 + i)
                        act.activation(y_hi[:, 512 * (i - 1):512 * i], B[4 + i][:, :], ACT.Copy).then_inc(y_hi_ready, 1)
                    job_hi(j + 1, i)
                take_turned(j + 1)

            act.wait_ge(routed, 1)
            n_over = act.value_load(over[0:1, 0:1], min_val=0, max_val=MAX_OVER)
            with act.Fori(0, n_over + N_EXP) as j:
                job(j)

            act.wait_ge(added, n_over * 4 + 4 * N_EXP + 1)
            token_squares(14)
            root(14, 2)

        @block.gpsimd
        def _(pool):
            rows = [("ev_g_q_lat", G_QL, 2), ("ev_g_kv_lat", G_KV, 1),
                    ("ev_norm_ffn", G_FFN0, 8), ("od_norm_mix", G_MIX1, 8), ("od_g_sub", G_SUB, 1),
                    ("od_norm_ffn", G_FFN1, 8)]
            for name, r, n in rows:
                pool.dma_start(gain_rows[r:r + n, :], a[name][0].rearrange("(c p) -> c p", p=P)).then_inc(small_landed, 16)
            pool.dma_start(rope[:, :, :], rope_in.rearrange("(b p) r -> p b r", p=P)).then_inc(small_landed, 16)
            pool.dma_start(g_idx, a["ev_g_idx_k"].to_broadcast([P, D_IDX])).then_inc(small_landed, 16)
            for k, name in enumerate(("od_lambda_q1", "od_lambda_k1", "od_lambda_q2", "od_lambda_k2")):
                pool.dma_start(lam_in[:, k], a[name].to_broadcast([P, DH])).then_inc(small_landed, 16)
            pool.memset(ones[:, :], 1.0).then_inc(ones_set, 1)
            pool.wait_ge(o_out, 8)
            pool.dma_start(wr[:, :, :], a["od_w_router"][0].rearrange("(c p) e -> p c e", p=P)).then_inc(late_landed, 16)
            pool.dma_start(final_gain[:, :], a["final_norm"].rearrange("(o d) -> o d", o=1).to_broadcast([P, D]))\
                .then_inc(late_landed, 16)

        @block.vector
        def _(dve):
            steps = [0]

            def link(ins):
                steps[0] += 1
                ins.then_inc(v_step, 1)
                dve.wait_ge(v_step, steps[0])

            def lo_part(i):
                size = size_of[i]
                dve.wait_ge(hi_ready, i + 1)
                dve.tensor_tensor(w_lo[:, i % HL, 0:size], raw[:, i % RAW, 0:size], w_hi[:, i % HL, 0:size].bitcast(F32),
                                  ALU.subtract).then_inc(lo_ready, 1)

            def job_lo(j, i):
                g = T_MOE + i
                dve.wait_ge(hi_ready, j * JOB + g + 1)
                dve.tensor_tensor(w_lo[:, g % HL, :], raw[:, g % RAW, :], w_hi[:, g % HL, :].bitcast(F32), ALU.subtract)\
                   .then_inc(lo_ready, 1)

            counts = {"squares": 0, "root": 0, "chunks": 0}

            def inverse_root(c0, n, squared, scale=1.0):
                counts["squares"] += squared
                dve.wait_ge(squares, counts["squares"])
                dve.tensor_scalar(stat[:, c0:c0 + n], stat[:, c0:c0 + n], scale, EPS, ALU.mult, ALU.add).then_inc(var_ready, 1)
                counts["root"] += 1
                dve.wait_ge(root_ready, counts["root"])
                link(dve.reciprocal(stat[:, c0:c0 + n], stat[:, c0:c0 + n]))

            def norm_tokens(c0):
                inverse_root(c0, 2, 2)
                for b in range(T):
                    dve.tensor_scalar(xn[:, b], x[:, b], stat[:, c0 + b:c0 + b + 1], None, ALU.mult).then_inc(src_ready, 1)

            def fill(gain, banks=4, chunks=8):
                for g in range(banks):
                    mine = [c for c in (2 * g, 2 * g + 1) if c < chunks]
                    counts["chunks"] += len(mine)
                    dve.wait_ge(fill_hi, counts["chunks"])
                    for c in mine:
                        scale = 1.0 if gain is None else gains[:, gain(c):gain(c) + 1]
                        dve.scalar_tensor_tensor(xt_lo[:, c, :], B[4 + g][:, (c % 2) * S:(c % 2 + 1) * S], scale,
                                                 xt_hi[:, c, :].bitcast(F32), ALU.mult, ALU.subtract).then_inc(fill_lo, 1)

            def unit(q, tile, out_ap):
                dve.wait_ge(tile_used, tile + 1)
                dve.tensor_copy(out_ap, B[2 * (q % 2) + 1][:, 0:out_ap.shape[-1]]).then_inc(unit_out[q], 1)

            def unit_to_x(q, tile, half):
                dve.wait_ge(tile_used, tile + 1)
                for b in range(T):
                    part = x[:, b, 512 * half:512 * half + 512]
                    dve.tensor_tensor(part, B[2 * (q % 2) + b][:, :], part, ALU.add).then_inc(unit_out[q], 1)

            def rotate(v, n, f, col):
                def table(c):
                    return rope[:, :, c:c + f].unsqueeze(2).to_broadcast([P, T, n, f])
                cos, sin = table(col), table(col + f)
                x1, x2 = v[:, :, :, 0:f], v[:, :, :, f:2 * f]
                t1, t2 = (sc[:, k, 0:T * n * f].rearrange("p (b n f) -> p b n f", b=T, n=n) for k in range(2))
                dve.tensor_tensor(t1, x1, sin, ALU.mult)
                dve.tensor_tensor(t2, x2, sin, ALU.mult)
                dve.tensor_tensor(x1, x1, cos, ALU.mult)
                link(dve.tensor_tensor(x2, x2, cos, ALU.mult))
                dve.tensor_tensor(x1, x1, t2, ALU.subtract)
                link(dve.tensor_tensor(x2, x2, t1, ALU.add))

            def turn(first, n, dst):
                for g in range(n):
                    if (first + g) % 2:
                        dve.wait_ge(turn_t, first + g + 1)
                        d, parts, width = dst(g)
                        dve.tensor_copy(d, B[(first + g) % 4][0:parts, 0:width]).then_inc(turn_v, 1)

            dve.wait_ge(gains_t, 1)
            dve.tensor_copy(gains[:, 0:8], B[7][:, 0:8]).then_inc(gains_ready, 1)
            dve.wait_ge(x_landed, 16)
            norm_tokens(0)
            lo_part(0)
            dve.wait_ge(gains_ready, 1)
            fill(lambda c: G_MIX0 + c)
            for i in range(1, HL):
                lo_part(i)
            for q in range(5):
                for i in (2 * q, 2 * q + 1):
                    if i >= HL:
                        lo_part(i)
                if q:
                    unit(q - 1, 2 * q - 1, z[:, 1, 512 * (q - 1):512 * q])
                if q == 1:
                    dve.wait_ge(gains_t, 2)
                    dve.tensor_copy(gains[:, 8:N_GAINS], B[7][:, 8:N_GAINS]).then_inc(gains_ready, 1)
                    dve.wait_ge(small_landed, 16 * 12)
                    for k in range(2):
                        dve.tensor_tensor_reduce(lam_in[:, 2 * k], lam_in[:, 2 * k], lam_in[:, 2 * k + 1], 1.0, 0.0, ALU.mult,
                                                 ALU.add, stat[:, LAM + k:LAM + k + 1]).then_inc(lam_dots, 1)
                    dve.wait_ge(gains_ready, 2)
            lo_part(T_UQ)
            unit(4, T_IN + 9, z[:, 1, 2048:IN_EVEN])
            lo_part(T_UKV)
            lo_part(T_OUT0)

            inverse_root(8, 6, 6)
            for b in range(T):
                dve.tensor_scalar(z[:, b, C_Q:C_Q + Q_LORA], z[:, b, C_Q:C_Q + Q_LORA], stat[:, 8 + b:9 + b], None, ALU.mult)
                dve.tensor_scalar(z[:, b, C_KV:C_KV + KV_LORA], z[:, b, C_KV:C_KV + KV_LORA], stat[:, 10 + b:11 + b], None,
                                  ALU.mult).then_inc(src_ready, 1)
            for b in range(T):
                link(dve.scalar_tensor_tensor(z[:, b, K_I:K_I + D_IDX], z[:, b, K_I:K_I + D_IDX], stat[:, 12 + b:13 + b],
                                              g_idx, ALU.mult, ALU.mult))
            rotate(z[:, :, Q_I:W_I].rearrange("p b (n d) -> p b n d", n=H + 1), H + 1, D_IDX // 8, R_4)
            dve.tensor_copy(z[:, :, K_REP:K_REP + P].rearrange("p b (r d) -> p b r d", r=4),
                            z[:, :, K_I:W_I].unsqueeze(2).to_broadcast([P, T, 4, D_IDX])).then_inc(rot_ready, 1)
            fill(lambda c: G_QL + c, banks=2, chunks=3)

            rotate(z[:, :, Q_B:V_B].rearrange("p b (n d) -> p b n d", n=2 * H), 2 * H, DH // 8, R_8)
            rotate(z[:, :, K_ROPE:Q_B].rearrange("p b (n d) -> p b n d", n=1), 1, ROPE_A // 2, R_16)
            dve.tensor_copy(ka[:, :, :, NOPE:], z[:, :, K_ROPE:Q_B].unsqueeze(2).to_broadcast([P, T, H, ROPE_A]))
            dve.wait_ge(tile_used, T_UQ + 1)
            q1 = qa[:, 1].rearrange("p h d -> p (h d)")
            dve.tensor_copy(q1[:, 0:512], B[3][:, :]).then_inc(unit_out[5], 1)
            dve.tensor_copy(q1[:, 512:768], B[1][:, 0:256]).then_inc(unit_out[6], 1)
            dve.wait_ge(tile_used, T_UKV + 1)
            for q in range(2):
                src = B[5 if q == 0 else 7].rearrange("p (h d) -> p h d", h=4)
                dve.tensor_copy(ka[:, 1, 4 * q:4 * q + 4, 0:NOPE], src[:, :, 0:NOPE]).then_inc(unit_out[7 + q], 1)
                dve.tensor_copy(z[:, 1, V_MLA + 256 * q:V_MLA + 256 * q + 256].rearrange("p (h d) -> p h d", h=4),
                                src[:, :, NOPE:]).then_inc(unit_out[7 + q], 1)
            for q in (5, 6):
                dve.wait_ge(unit_out[q], 2)
            rotate(qa[:, :, :, NOPE:], H, ROPE_A // 2, R_16)
            dve.engine_nop().then_inc(rot_ready, 1)

            turn(0, 2, turn_idx)
            turn(2, 8, turn_a)
            for u in range(2 * H):
                b, h = u // H, u % H
                nk = P * (b + 1)
                dve.wait_ge(ix_relu, u + 1)
                if h:
                    dve.wait_ge(ix_sum, u)
                dve.scalar_tensor_tensor(key_mask[:, b, 0:nk], sc[:, u % 3, 0:nk], z[:, b, W_I + h:W_I + h + 1],
                                         key_mask[:, b, 0:nk] if h else hidden[b], ALU.mult, ALU.add).then_inc(ix_sum, 1)
            dve.wait_ge(ix_sum, 2 * H)

            def top_k(i):
                b, nk = i // H, P * (i // H + 1)
                work = key_mask[:, b, 0:nk]
                link(dve.max(top8[:, :], work))
                link(dve.match_replace(work, top8[:, :], work, TAKEN))
                if i % H == TOP_K // 8 - 1:
                    link(dve.tensor_scalar(work, work, TAKEN / 2, NEG, ALU.is_gt, ALU.mult))

            def attend(u0, maps, scale, mask, leave, group, beside=None):
                n = 2 * H
                for i in range(n + 4):
                    u = u0 + i
                    if i < n:
                        b, nk = i // H, P * (i // H + 1)
                        dve.wait_ge(scores, u + 1)
                        if u >= 3:
                            dve.wait_ge(exps, u - 2)
                        for c in range(maps):
                            t = dve.tensor_tensor_reduce(sc[:, u % 3, c * S:c * S + nk], B[score_bank(u, c, maps)][:, 0:nk], mask[b],
                                                         -scale, 3e38, ALU.add, ALU.min, peak[:, u % 3, c:c + 1])
                        t.then_inc(masked, 1)
                        if beside:
                            beside(i)
                    if maps == 2 and 1 <= i <= n:
                        v = u - 1
                        b, nk = (i - 1) // H, P * ((i - 1) // H + 1)
                        k = 2 * n + 2 * (i - 1)
                        dve.wait_ge(exps, v + 1)
                        link(dve.reciprocal(recip[:, 0:1], sums[:, k + 1:k + 2]))
                        link(dve.scalar_tensor_tensor(recip[:, 1:2], sums[:, k:k + 1], recip[:, 0:1],
                                                      stat[:, NEG_LAM:NEG_LAM + 1], ALU.mult, ALU.mult))
                        dve.scalar_tensor_tensor(pr[:, v % 3, 0:nk], pr[:, v % 3, S:S + nk], recip[:, 1:2],
                                                 pr[:, v % 3, 0:nk], ALU.mult, ALU.add).then_inc(mixed, 1)
                    e = i - 3
                    if 0 <= e < n and e % group == group - 1:
                        dve.wait_ge(pv, u0 + e + 1)
                        leave(e // group)

            def leave_mla(g, dst, first, bank):
                k = first + H * g
                link(dve.reciprocal(recip[:, 0:8], sums[:, k:k + 8]))
                dve.tensor_tensor(dst(g).rearrange("p (h d) -> p h d", h=H), B[bank][:, :].rearrange("p (h d) -> p h d", h=H),
                                  recip[:, 0:8].unsqueeze(2).to_broadcast([P, H, DH]), ALU.mult).then_inc(o_out, 1)

            attend(0, 1, (NOPE + ROPE_A) ** -0.5, hidden, lambda g: leave_mla(g, lambda b: o_a[:, b], 0, 5 + g), H, top_k)
            dve.wait_ge(lam_exp, 1)
            link(dve.tensor_tensor(stat[:, LAM + 2:LAM + 3], stat[:, LAM + 1:LAM + 2], stat[:, LAM:LAM + 1], ALU.subtract))
            link(dve.tensor_scalar(stat[:, NEG_LAM:NEG_LAM + 1], stat[:, LAM + 2:LAM + 3], -LAMBDA_INIT, None, ALU.add))
            turn(10, 4, turn_b)
            attend(2 * H, 1, DH ** -0.5, [key_mask[:, 0, 0:P], key_mask[:, 1, :]],
                   lambda g: leave_mla(g, lambda b: z[:, b, Q_B:K_B], 2 * H, 5 + g), H)
            for i in (T_OUT0 + 1, T_OUT0 + 2):
                lo_part(i)
            fill(None)
            lo_part(T_OUT0 + 3)
            unit_to_x(9, T_OUT0 + 1, 0)
            lo_part(T_FFN)
            lo_part(T_FFN + 1)
            unit_to_x(10, T_OUT0 + 3, 1)

            for q in (9, 10):
                dve.wait_ge(unit_out[q], 2)
            norm_tokens(2)
            fill(lambda c: G_FFN0 + c)
            lo_part(T_FFN + 2)

            def add_down(n, tiles):
                for half in range(2):
                    dve.wait_ge(tile_used, T_FFN + tiles[min(half, len(tiles) - 1)] + 1)
                    for b in range(T):
                        k = 4 * n + 2 * half + b
                        if k >= 4:
                            dve.wait_ge(f_add, k - 3)
                        part = x[:, b, 512 * half:512 * half + 512]
                        dve.tensor_tensor(part, B[down_bank(k)][:, :], part, ALU.add).then_inc(f_add, 1)
                    yield

            for n in range(FFN_STEPS + 1):
                g, u, d = ffn_tiles(n)
                w = 512 if n < FFN_STEPS - 1 else 256
                adds = add_down(n - 2, ffn_tiles(n - 1)[2]) if n >= 2 else iter(())
                for i in g:
                    if i > 2:
                        lo_part(T_FFN + i)
                    next(adds, None)
                for _ in adds:
                    pass
                for i in u:
                    if i > 2:
                        lo_part(T_FFN + i)
                if n == FFN_STEPS:
                    for i in d:
                        lo_part(T_FFN + i)
                if d:
                    c = 4 if n < FFN_STEPS else 2
                    for b in range(T):
                        dve.wait_ge(f_thi, 2 * (n - 1) + b + 1)
                        dve.tensor_tensor(ht_lo[:, 0:c, b * P:b * P + P], B[4][:, 0:c * P].rearrange("p (c t) -> p c t", c=c),
                                          ht_hi[:, 0:c, b * P:b * P + P].bitcast(F32), ALU.subtract).then_inc(f_tlo, 1)
                    if n < FFN_STEPS:
                        for i in d:
                            lo_part(T_FFN + i)
                if g:
                    dve.wait_ge(tile_used, T_FFN + u[-1] + 1)
                    for b in range(T):
                        dve.wait_ge(f_silu, 2 * n + b + 1)
                        if n:
                            dve.wait_ge(f_t, 2 * n)
                        dve.tensor_tensor(hh[:, b, 0:w], sg[:, b, 0:w], B[2 + b][:, 0:w], ALU.mult).then_inc(f_h, 1)
            lo_part(T_QKV)
            lo_part(T_QKV + 1)
            for _ in add_down(FFN_STEPS - 1, ffn_tiles(FFN_STEPS)[2]):
                pass

            dve.wait_ge(f_add, 4 * FFN_STEPS)
            norm_tokens(4)
            fill(lambda c: G_MIX1 + c)
            lo_part(T_QKV + 2)
            for q in range(6):
                for i in (2 * q, 2 * q + 1):
                    if i >= HL:
                        lo_part(T_QKV + i)
                if q:
                    unit(11 + q - 1, T_QKV + 2 * q - 1, z[:, 1, 512 * (q - 1):512 * q])
            lo_part(T_OUT1)
            unit(16, T_QKV + 11, z[:, 1, 2560:3072])
            for q in range(11, 15):
                dve.wait_ge(unit_out[q], 2)
            rotate(z[:, :, 0:2048].rearrange("p b (n d) -> p b n d", n=4 * H), 4 * H, DH // 8, R_8)
            dve.engine_nop().then_inc(rot_ready, 1)
            turn(14, 8, turn_c)

            def leave_diff(g):
                b, half = g // 2, g % 2
                k = 4 * H + 2 * (H * b + 4 * half)
                link(dve.reciprocal(recip[:, 4:8], sums[:, k:k + 8].rearrange("p (h c) -> p h c", c=2)[:, :, 0]))
                o = z[:, b, 512 * half:512 * half + 512].rearrange("p (h d) -> p h d", h=4)
                link(dve.tensor_tensor(o, B[5 + g % 2][:, :].rearrange("p (h d) -> p h d", h=4),
                                       recip[:, 4:8].unsqueeze(2).to_broadcast([P, 4, 2 * DH]), ALU.mult))
                sq = o_a[:, 0].rearrange("p (h d) -> p h d", h=4)
                link(dve.tensor_tensor(sq, o, o, ALU.mult))
                c = HEAD_MS + H * b + 4 * half
                dve.tensor_reduce(stat[:, c:c + 4], sq, AX.X, ALU.add).then_inc(o_out, 1)

            attend(4 * H, 2, DH ** -0.5, hidden, leave_diff, 4)
            dve.wait_ge(o_out, 8)
            inverse_root(HEAD_MS, 2 * H, 0, scale=1.0 / (2 * DH))
            for b in range(T):
                o = z[:, b, 0:D].rearrange("p (h d) -> p h d", h=H)
                dve.scalar_tensor_tensor(o, o, 1.0 - LAMBDA_INIT,
                                         stat[:, HEAD_MS + H * b:HEAD_MS + H * b + H].unsqueeze(2).to_broadcast([P, H, 2 * DH]),
                                         ALU.mult, ALU.mult).then_inc(src_ready, 1)
            for i in (T_OUT1 + 1, T_OUT1 + 2):
                lo_part(i)
            fill(lambda c: G_SUB)
            lo_part(T_OUT1 + 3)
            unit_to_x(17, T_OUT1 + 1, 0)
            dve.wait_ge(wr_split, 1)
            dve.tensor_tensor(wr_lo[:, :, :], wr[:, :, :], wr_hi[:, :, :].bitcast(F32), ALU.subtract).then_inc(wr_split_lo, 1)
            unit_to_x(18, T_OUT1 + 3, 1)

            for q in (17, 18):
                dve.wait_ge(unit_out[q], 2)
            norm_tokens(6)
            fill(lambda c: G_FFN1 + c)

            def select(j):
                dve.tensor_copy(place_now[:, :], place[:, :, bass.ds(j, 1)].rearrange("p b o -> p (b o)")).then_inc(place_copied, 1)
                dve.wait_ge(place_copied, j + 1)
                for b in range(T):
                    e = dve.tensor_scalar(sel[:, b, :], iota, place_now[:, b:b + 1], None, ALU.is_equal)
                e.then_inc(sel_ready, 1)

            def take_gathered(j):
                for k in range(2):
                    dve.wait_ge(xg_hi_ready, j * 2 + k + 1)
                    for c in range(4 * k, 4 * k + 4):
                        e = dve.scalar_tensor_tensor(xg_lo[:, c, :], B[1 + 2 * k][:, (c % 4) * P:(c % 4 + 1) * P],
                                                     gains[:, G_FFN1 + c:G_FFN1 + c + 1], xg_hi[:, c, :].bitcast(F32),
                                                     ALU.mult, ALU.subtract)
                e.then_inc(xg_lo_ready, 1)

            def small(c, n=16):
                return moe_s[:, c:c + n]

            def pair(c):
                return small(c).rearrange("p (b e) -> p b e", b=T)

            lg, top, gap, pick = pair(0), pair(16), small(32, 2), small(40, 4).rearrange("p (b k) -> p b k", b=T)
            chose, mix, tmp, spot, pick_0 = pair(48), pair(64), pair(80), pair(96), pair(184)
            cnt, ov, cum, rank, number = (small(c, 8) for c in (112, 120, 128, 136, 168))
            this, over_e = (over_s[:, c:c + 24].rearrange("p (o e) -> p o e", o=MAX_OVER) for c in (0, 24))
            over_place, over_gate = (over_s[:, c:c + 48].rearrange("p (b o e) -> p b o e", b=T, o=MAX_OVER) for c in (48, 96))
            dve.wait_ge(logits_t, 1)
            dve.tensor_copy(logit_rows, B[0][0:N_EXP, 0:S]).then_inc(logits_out, 1)
            dve.wait_ge(logits, 1)
            link(dve.tensor_copy(lg, B[6][:, 0:16].rearrange("p (b e) -> p b e", b=T)))
            for b in range(T):
                link(dve.max(top[:, b], lg[:, b]))
                link(dve.max_index(top_i[:, b], top[:, b], lg[:, b]))
            dve.tensor_copy(pick, top_i[:, :, 0:2])
            link(dve.tensor_tensor(gap, top[:, :, 1], top[:, :, 0], ALU.subtract))
            for b in range(T):
                dve.tensor_scalar(pick_0[:, b], iota_e, pick[:, b, 0:1], None, ALU.is_equal)
                link(dve.tensor_scalar(tmp[:, b], iota_e, pick[:, b, 1:2], None, ALU.is_equal))
            dve.tensor_tensor(chose, pick_0, tmp, ALU.add).then_inc(chosen, 1)
            for b in range(T):
                dve.wait_ge(xn_split, b + 1)
                dve.tensor_tensor(xn_lo[:, b], xn[:, b], xn_hi[:, b].bitcast(F32), ALU.subtract).then_inc(xn_split_lo, 1)
            dve.wait_ge(places, 1)
            for b in range(T):
                link(dve.tensor_scalar(spot[:, b], B[7][:, 8 * b:8 * b + 8], 1.0, None, ALU.add))
            link(dve.tensor_copy(cnt, B[7][:, 16:24]))
            link(dve.tensor_tensor(spot, spot, chose, ALU.mult))
            link(dve.memset(place[:, :, :], -1.0))
            link(dve.memset(gate[:, :, :], 0.0))
            link(dve.tensor_scalar(place[:, :, 0:8], spot, -1.0, None, ALU.add))
            select(0)
            for i in range(AHEAD):
                job_lo(0, i)
            dve.wait_ge(gate_exp, 1)
            link(dve.tensor_scalar(small(34, 2), gap, 1.0, None, ALU.add))
            link(dve.reciprocal(small(36, 2), small(34, 2)))
            for b in range(T):
                link(dve.scalar_tensor_tensor(mix[:, b], tmp[:, b], moe_s[:, 32 + b:33 + b], pick_0[:, b], ALU.mult, ALU.add))
                link(dve.tensor_scalar(mix[:, b], mix[:, b], moe_s[:, 36 + b:37 + b], None, ALU.mult))
            dve.tensor_copy(gate[:, :, 0:8], mix)
            take_gathered(0)
            link(dve.tensor_scalar(ov, cnt, float(P), None, ALU.is_gt))
            link(dve.tensor_tensor_scan(cum, ones[:, 0:8], ov, 0.0, ALU.mult, ALU.add))
            link(dve.tensor_tensor(rank, cum, ov, ALU.mult))
            link(dve.memset(number, 0.0))
            dve.tensor_copy(number[:, 0:1], cum[:, 7:8])
            for o in range(MAX_OVER):
                e = dve.tensor_scalar(this[:, o], rank, float(o + 1), None, ALU.is_equal)
            link(e)
            for b in range(T):
                dve.tensor_tensor(over_place[:, b], this, spot[:, b].unsqueeze(1).to_broadcast([P, MAX_OVER, 8]), ALU.mult)
                dve.tensor_tensor(over_gate[:, b], this, mix[:, b].unsqueeze(1).to_broadcast([P, MAX_OVER, 8]), ALU.mult)
            link(dve.tensor_tensor(over_e, this, iota_e.unsqueeze(1).to_broadcast([P, MAX_OVER, 8]), ALU.mult))
            dve.tensor_reduce(place[:, :, N_EXP:N_EXP + MAX_OVER], over_place, AX.X, ALU.add)
            dve.tensor_reduce(gate[:, :, N_EXP:N_EXP + MAX_OVER], over_gate, AX.X, ALU.add)
            link(dve.tensor_reduce(number[:, 1:1 + MAX_OVER], over_e, AX.X, ALU.add))
            link(dve.tensor_scalar(place[:, :, N_EXP:N_EXP + MAX_OVER], place[:, :, N_EXP:N_EXP + MAX_OVER], -1.0 - P, None, ALU.add))
            dve.tensor_copy(over[:, :], number[:, 0:5]).then_inc(routed, 1)

            dve.wait_ge(routed, 1)
            dve.engine_nop().then_inc(added, 1)

            def job(j):
                for n in range(E_STEPS + 1):
                    g, u, d = job_tiles(n)
                    for i in g + u:
                        if i >= AHEAD:
                            job_lo(j, i)
                    if n == E_STEPS:
                        for i in d:
                            job_lo(j, i)
                    if d:
                        dve.wait_ge(m_thi, j * E_STEPS + n)
                        dve.tensor_tensor(ht_lo[:, :, 0:P], B[4].rearrange("p (c t) -> p c t", c=4),
                                          ht_hi[:, :, 0:P].bitcast(F32), ALU.subtract).then_inc(m_tlo, 1)
                    if d and n < E_STEPS:
                        for i in d:
                            job_lo(j, i)
                    if g:
                        dve.wait_ge(tile_used, j * JOB + T_MOE + u[-1] + 1)
                        dve.wait_ge(m_silu, j * E_STEPS + n + 1)
                        if n:
                            dve.wait_ge(m_t, j * E_STEPS + n)
                        dve.tensor_tensor(hh[:, 0], sg[:, 0], B[2][:, :], ALU.mult).then_inc(m_h, 1)
                    if n == 3:
                        dve.wait_ge(sel_turned, j + 1)
                        dve.tensor_copy(gate_now[:, :], gate[:, :, bass.ds(j, 1)].rearrange("p b o -> p (b o)"))
                        select(j + 1)
                take_gathered(j + 1)
                job_lo(j + 1, 0)
                for k in range(2):
                    dve.wait_ge(y_hi_ready, j * 2 + k + 1)
                    dve.tensor_tensor(y_lo[:, 512 * k:512 * k + 512], B[5 + k][:, :],
                                      y_hi[:, 512 * k:512 * k + 512].bitcast(F32), ALU.subtract).then_inc(y_lo_ready, 1)
                for k in range(4):
                    b, half = k % 2, k // 2
                    part = x[:, b, 512 * half:512 * half + 512]
                    dve.wait_ge(scattered, j * 4 + k + 1)
                    if k == 0:
                        dve.wait_ge(added, j * 4 + 1)
                    dve.scalar_tensor_tensor(part, B[SCATTER_BANKS[k]][:, :], gate_now[:, b:b + 1], part, ALU.mult, ALU.add)\
                       .then_inc(added, 1)
                    if k == 0:
                        job_lo(j + 1, 1)
                job_lo(j + 1, 2)

            n_over = dve.value_load(over[0:1, 0:1], min_val=0, max_val=MAX_OVER)
            with dve.Fori(0, n_over + N_EXP) as j:
                job(j)

            inverse_root(14, 2, 2)
            dve.wait_ge(late_landed, 32)
            for b in range(T):
                dve.scalar_tensor_tensor(x[:, b], x[:, b], stat[:, 14 + b:15 + b], final_gain[:, :], ALU.mult, ALU.mult)\
                   .then_inc(done, 1)

        @block.tensor
        def _(pe):
            def three(out_ap, l_hi, l_lo, r_hi, r_lo, first, last):
                pe.matmul(out_ap, l_hi, r_hi, start=first, stop=False)
                pe.matmul(out_ap, l_hi, r_lo, start=False, stop=False)
                return pe.matmul(out_ap, l_lo, r_hi, start=False, stop=last)

            def w_part(i, c, width, c0=0, n=None):
                n = width if n is None else n
                return (w_hi[:, i % HL, c * width + c0:c * width + c0 + n], w_lo[:, i % HL, c * width + c0:c * width + c0 + n])

            banks_filled = [0]
            chunks_filled = [0]

            def fill(source, chunks=8):
                for g in range((chunks + 1) // 2):
                    mine = [c for c in (2 * g, 2 * g + 1) if c < chunks]
                    for c in mine:
                        for b in range(T):
                            m = pe.transpose(B[4 + g][:, (c % 2) * S + b * P:(c % 2) * S + b * P + P], source(b, c), ident)
                    m.then_inc(fill_t, 1)
                chunks_filled[0] += chunks

            def chunk_filled(kc, first):
                if first:
                    pe.wait_ge(fill_lo, chunks_filled[0] - KC + kc + 1)

            def unit(q, tile, width, first=False):
                for half in range(2):
                    pe.wait_ge(lo_ready, tile + half + 1)
                    for b in range(T):
                        for c in range(4):
                            kc = 4 * half + c
                            chunk_filled(kc, first and b == 0)
                            m = three(B[2 * (q % 2) + b][:, 0:width], xt_hi[:, kc, b * P:b * P + P], xt_lo[:, kc, b * P:b * P + P],
                                      *w_part(tile + half, c, width), kc == 0, kc == KC - 1)
                    m.then_inc(tile_used, 1)

            pe.wait_ge(cst_landed, 16)
            pe.wait_ge(mix_landed, 16)
            pe.transpose(B[7][:, 0:8], gain_rows[0:8, :], ident[0:8, 0:8]).then_inc(gains_t, 1)
            pe.wait_ge(gains_ready, 1)

            pe.wait_ge(src_ready, 2)
            fill(lambda b, c: xn[:, b, c * P:c * P + P])
            for q in range(5):
                if q >= 2:
                    pe.wait_ge(unit_out[q - 2], 2)
                unit(q, 2 * q, min(512, IN_EVEN - 512 * q), q == 0)
                if q == 0:
                    pe.wait_ge(small_landed, 16 * 12)
                    pe.transpose(B[7][:, 0:N_GAINS], gain_rows[:, :], ident[0:N_GAINS, 0:N_GAINS]).then_inc(gains_t, 1)
            for q in (3, 4):
                pe.wait_ge(unit_out[q], 2)
            pe.wait_ge(src_ready, 4)
            fill(lambda b, c: z[:, b, c * P:c * P + P], chunks=3)
            pe.wait_ge(fill_lo, chunks_filled[0])
            pe.wait_ge(lo_ready, T_UQ + 1)
            for b in range(T):
                for bank, c0, n in ((2, 0, 512), (0, 512, 256)):
                    for c in range(2):
                        m = three(B[bank + b][:, 0:n], xt_hi[:, c, b * P:b * P + P], xt_lo[:, c, b * P:b * P + P],
                                  *w_part(T_UQ, c, 768, c0, n), c == 0, c == 1)
            m.then_inc(tile_used, 1)
            pe.wait_ge(lo_ready, T_UKV + 1)
            for b in range(T):
                for half in range(2):
                    m = three(B[4 + 2 * half + b][:, :], xt_hi[:, 2, b * P:b * P + P], xt_lo[:, 2, b * P:b * P + P],
                              *w_part(T_UKV, 0, 1024, 512 * half, 512), True, True)
            m.then_inc(tile_used, 1)

            def turn(first, n, source, parts=P):
                for g in range(n):
                    G = first + g
                    if G >= 4:
                        pe.wait_ge(turn_v if G % 2 else turn_s, (G - 4) // 2 + 1)
                    for k, ap in enumerate(source(g)):
                        m = pe.transpose(B[G % 4][0:parts, k * P:k * P + P], ap, ident)
                    m.then_inc(turn_t, 1)

            def heads_a(g):
                src = (qa, ka)[g // 4]
                return [src[:, b, h, :] for h in (2 * (g % 4), 2 * (g % 4) + 1) for b in range(T)]

            pe.wait_ge(rot_ready, 1)
            for q in (5, 6):
                pe.wait_ge(unit_out[q], 2)
            turn(0, 2, lambda g: [z[:, b, Q_I + c * P:Q_I + c * P + P] for c in range(2) for b in range(T)] if g == 0
                 else [z[:, b, K_REP:K_REP + P] for b in range(T)])
            pe.wait_ge(rot_ready, 2)
            for q in (7, 8):
                pe.wait_ge(unit_out[q], 4)
            turn(2, 8, heads_a, NOPE + ROPE_A)
            pe.wait_ge(turn_s, 5)
            pe.wait_ge(turn_v, 5)
            for u in range(2 * H):
                b, h = u // H, u % H
                r = 32 * (h % 4)
                if u >= 3:
                    pe.wait_ge(ix_relu, u - 2)
                pe.matmul(B[u % 3][:, 0:P * (b + 1)], idx_t[r:r + 32, h // 4, b * P:b * P + P],
                          idx_t[r:r + 32, 2, 0:P * (b + 1)], start=True, stop=True).then_inc(ix_dots, 1)
            pe.wait_ge(ix_relu, 2 * H)

            def attend(u0, maps, q_of, k_of, v_of, width, group, g0):
                n = 2 * H
                for i in range(n + 3):
                    u = u0 + i
                    if i < n:
                        b, h, nk = i // H, i % H, P * (i // H + 1)
                        if u >= 3:
                            pe.wait_ge(masked, u - 1 if maps == 2 else u - 2)
                        for c in range(maps):
                            m = pe.matmul(B[score_bank(u, c, maps)][:, 0:nk], q_of(h, c)[:, b * P:b * P + P], k_of(h, c)[:, 0:nk],
                                          start=True, stop=True)
                        m.then_inc(scores, 1)
                    if 2 <= i < n + 2:
                        v, b = u - 2, (i - 2) // H
                        pe.wait_ge(mixed if maps == 2 else exps, v + 1 - (u0 if maps == 2 else 0))
                        if v >= 2:
                            pe.wait_ge(probs_out, v - 1)
                        for k in range(b + 1):
                            m = pe.transpose(B[3 + v % 2][:, k * P:k * P + P], pr[:, v % 3, k * P:k * P + P], ident)
                        m.then_inc(probs_t, 1)
                    if i >= 3:
                        v, b, h = u - 3, (i - 3) // H, (i - 3) % H
                        g = g0 + (i - 3) // group
                        pe.wait_ge(probs_out, v + 1)
                        if g >= 2 and (i - 3) % group == 0:
                            pe.wait_ge(o_out, g - 1)
                        for k in range(b + 1):
                            c0 = (i - 3) % group * width
                            m = pe.matmul(B[5 + g % 2][:, c0:c0 + width], pt[:, v % 2, k, :], v_of(k, h), start=(k == 0), stop=(k == b))
                        m.then_inc(pv, 1)

            attend(0, 1, lambda h, c: qk_t[0:NOPE + ROPE_A, 0, h, :], lambda h, c: qk_t[0:NOPE + ROPE_A, 1, h, :],
                   lambda k, h: z[:, k, V_MLA + V_A * h:V_MLA + V_A * h + V_A], V_A, H, 0)
            pe.wait_ge(masked, 2 * H)
            turn(10, 4, lambda g: [z[:, b, (Q_B, K_B)[g // 2] + c * P:(Q_B, K_B)[g // 2] + c * P + P]
                                   for c in (2 * (g % 2), 2 * (g % 2) + 1) for b in range(T)])
            pe.wait_ge(turn_s, 7)
            pe.wait_ge(turn_v, 7)

            def head(qk, h, c):
                return qk_t[DH * (h % 2):DH * (h % 2) + DH, qk, h // 2, :]

            attend(2 * H, 1, lambda h, c: head(0, h, c), lambda h, c: head(1, h, c),
                   lambda k, h: z[:, k, V_B + DH * h:V_B + DH * h + DH], DH, H, 2)
            pe.wait_ge(o_out, 4)
            fill(lambda b, c: o_a[:, b, c * P:c * P + P] if c < 4 else z[:, b, Q_B + (c - 4) * P:Q_B + (c - 3) * P])
            for q in range(2):
                unit(9 + q, T_OUT0 + 2 * q, 512, q == 0)

            pe.wait_ge(src_ready, 6)
            fill(lambda b, c: xn[:, b, c * P:c * P + P])

            def ffn_products(tiles, bank, w):
                per = KC // len(tiles)
                for k, i in enumerate(tiles):
                    pe.wait_ge(lo_ready, T_FFN + i + 1)
                    for b in range(T):
                        for c in range(per):
                            kc = per * k + c
                            chunk_filled(kc, tiles[0] == 0 and b == 0)
                            m = three(B[bank + b][:, 0:w], xt_hi[:, kc, b * P:b * P + P], xt_lo[:, kc, b * P:b * P + P],
                                      *w_part(T_FFN + i, c, w), kc == 0, kc == KC - 1)
                    m.then_inc(tile_used, 1)
                    yield

            def ffn_turn(n, b):
                pe.wait_ge(f_h, 2 * n + b + 1)
                k = 2 * n + b
                if k:
                    pe.wait_ge(f_tlo, k)
                for c in range(4 if n < FFN_STEPS - 1 else 2):
                    m = pe.transpose(B[4][:, c * P:c * P + P], hh[:, b, c * P:c * P + P], ident)
                m.then_inc(f_t, 1)

            for n in range(FFN_STEPS + 1):
                g, u, d = ffn_tiles(n)
                w = 512 if n < FFN_STEPS - 1 else 256
                if g:
                    if n:
                        pe.wait_ge(f_silu, 2 * n)
                    for _ in ffn_products(g, 0, w):
                        pass
                if d:
                    ffn_turn(n - 1, 0)
                if u:
                    if n:
                        pe.wait_ge(f_h, 2 * n)
                    for k, _ in enumerate(ffn_products(u, 2, w)):
                        if k == 0 and d:
                            ffn_turn(n - 1, 1)
                elif d:
                    ffn_turn(n - 1, 1)
                if d:
                    pe.wait_ge(f_tlo, 2 * n)
                    fs = 4 if n < FFN_STEPS else 2
                    for half in range(2):
                        i = d[min(half, len(d) - 1)]
                        pe.wait_ge(lo_ready, T_FFN + i + 1)
                        for b in range(T):
                            k = 4 * (n - 1) + 2 * half + b
                            if k >= 3 and down_bank(k) == 5 + k % 3:
                                pe.wait_ge(f_add, k - 2)
                            for c in range(fs):
                                r = w_part(T_FFN + i, c, 512) if n < FFN_STEPS else w_part(T_FFN + i, c, 1024, 512 * half, 512)
                                m = three(B[down_bank(k)][:, :], ht_hi[:, c, b * P:b * P + P], ht_lo[:, c, b * P:b * P + P], *r,
                                          c == 0, c == fs - 1)
                        if half == 1 or len(d) == 2:
                            m.then_inc(tile_used, 1)

            pe.wait_ge(src_ready, 8)
            fill(lambda b, c: xn[:, b, c * P:c * P + P])
            for q in range(6):
                if q >= 2:
                    pe.wait_ge(unit_out[11 + q - 2], 2)
                unit(11 + q, T_QKV + 2 * q, 512, q == 0)
            pe.wait_ge(rot_ready, 3)
            for q in (15, 16):
                pe.wait_ge(unit_out[q], 2)
            turn(14, 8, lambda g: [z[:, b, D * (g // 4) + c * P:D * (g // 4) + c * P + P]
                                   for c in (2 * (g % 4), 2 * (g % 4) + 1) for b in range(T)])
            pe.wait_ge(turn_s, 11)
            pe.wait_ge(turn_v, 11)
            attend(4 * H, 2, lambda h, c: qk_t[DH * c:DH * c + DH, 0, h, :], lambda h, c: qk_t[DH * c:DH * c + DH, 1, h, :],
                   lambda k, h: z[:, k, 2 * D + 2 * DH * h:2 * D + 2 * DH * h + 2 * DH], 2 * DH, 4, 4)
            pe.wait_ge(src_ready, 10)
            fill(lambda b, c: z[:, b, c * P:c * P + P])
            for q in range(2):
                unit(17 + q, T_OUT1 + 2 * q, 512, q == 0)

            pe.wait_ge(src_ready, 12)
            fill(lambda b, c: xn[:, b, c * P:c * P + P])
            pe.wait_ge(wr_split_lo, 1)
            for c in range(KC):
                chunk_filled(c, True)
                m = three(B[0][0:N_EXP, 0:S], wr_hi[:, c, :], wr_lo[:, c, :], xt_hi[:, c, :], xt_lo[:, c, :], c == 0, c == KC - 1)
            m.then_inc(logits_t, 1)
            pe.wait_ge(logits_out, 1)
            for b in range(T):
                m = pe.transpose(B[6][:, 8 * b:8 * b + 8], logit_rows[:, b * P:b * P + P], ident[0:N_EXP, 0:N_EXP])
            m.then_inc(logits, 1)
            pe.wait_ge(chosen, 1)
            pe.wait_ge(ones_set, 1)
            m0, m1 = moe_s[:, 48:56], moe_s[:, 56:64]
            pe.matmul(B[7][:, 0:8], tri, m0, start=True, stop=True)
            pe.matmul(B[7][:, 8:16], tri, m1, start=True, stop=False)
            pe.matmul(B[7][:, 8:16], ones[:, :], m0, start=False, stop=True)
            pe.matmul(B[7][:, 16:24], ones[:, :], m0, start=True, stop=False)
            pe.matmul(B[7][:, 16:24], ones[:, :], m1, start=False, stop=True).then_inc(places, 1)

            def gather(j, half):
                if half == 0:
                    pe.wait_ge(sel_ready, j + 1)
                for c in range(4 * half, 4 * half + 4):
                    dst = B[1 + 2 * (c // 4)][:, (c % 4) * P:(c % 4 + 1) * P]
                    for k, (b, part) in enumerate([(b, part) for b in range(T) for part in (xn_hi, xn_lo)]):
                        m = pe.matmul(dst, part[:, b, c * P:c * P + P], sel[:, b, :], start=(k == 0), stop=(k == 3))
                m.then_inc(gathered, 1)

            def turn_sel():
                for b in range(T):
                    m = pe.matmul(B[7][:, b * P:b * P + P], sel[:, b, :], ident_r[:, :], start=True, stop=True)
                m.then_inc(sel_turned, 1)

            pe.wait_ge(xn_split_lo, 2)
            gather(0, 0)
            gather(0, 1)
            pe.wait_ge(wr_split, 2)
            pe.wait_ge(routed, 1)
            turn_sel()

            def job(j):
                def products(tiles, bank):
                    for k, i in enumerate(tiles):
                        g = T_MOE + i
                        pe.wait_ge(lo_ready, j * JOB + g + 1)
                        for c in range(4):
                            kc = 4 * k + c
                            m = three(B[bank][:, :], xg_hi[:, kc, :], xg_lo[:, kc, :], *w_part(g, c, 512), kc == 0, kc == KC - 1)
                        m.then_inc(tile_used, 1)

                pe.wait_ge(xg_lo_ready, j + 1)
                for n in range(E_STEPS + 1):
                    g, u, d = job_tiles(n)
                    if g:
                        if n:
                            pe.wait_ge(m_silu, j * E_STEPS + n)
                        products(g, 0)
                    if n == E_STEPS:
                        gather(j + 1, 0)
                    if d:
                        pe.wait_ge(m_h, j * E_STEPS + n)
                        if n == 1:
                            pe.wait_ge(added, j * 4 + 1)
                        else:
                            pe.wait_ge(m_tlo, j * E_STEPS + n - 1)
                        for c in range(4):
                            m = pe.transpose(B[4][:, c * P:c * P + P], hh[:, 0, c * P:c * P + P], ident)
                        m.then_inc(m_t, 1)
                    if n == E_STEPS:
                        gather(j + 1, 1)
                    if u:
                        if n:
                            pe.wait_ge(m_h, j * E_STEPS + n)
                        products(u, 2)
                    if d:
                        pe.wait_ge(m_tlo, j * E_STEPS + n)
                        for half, i in enumerate(d):
                            k = T_MOE + i
                            pe.wait_ge(lo_ready, j * JOB + k + 1)
                            for c in range(4):
                                m = three(B[5 + half][:, :], ht_hi[:, c, 0:P], ht_lo[:, c, 0:P], *w_part(k, c, 512),
                                          n == 1 and c == 0, n == E_STEPS and c == 3)
                            m.then_inc(tile_used, 1)
                pe.wait_ge(sel_t_ready, j + 1)
                for k in range(4):
                    b, half = k % 2, k // 2
                    pe.wait_ge(y_lo_ready, j * 2 + half + 1)
                    for part in (y_hi, y_lo):
                        m = pe.matmul(B[SCATTER_BANKS[k]][:, :], sel_t[:, b * P:b * P + P], part[:, 512 * half:512 * half + 512],
                                      start=(part is y_hi), stop=(part is y_lo))
                    m.then_inc(scattered, 1)
                pe.wait_ge(added, j * 4 + 2)
                turn_sel()

            n_over = pe.value_load(over[0:1, 0:1], min_val=0, max_val=MAX_OVER)
            with pe.Fori(0, n_over + N_EXP) as j:
                job(j)
    return nc


SCATTER_BANKS = [7, 4, 5, 6]


def score_bank(u, c, maps):
    return u % 3 if maps == 1 else (0, 1, 2, 7)[2 * (u % 2) + c]


def down_bank(k):
    return 0 if k == 4 * FFN_STEPS - 1 else 5 + k % 3


_INS = ["x", "ev_norm_mix", "ev_w_in", "ev_g_q_lat", "ev_w_uq", "ev_g_kv_lat", "ev_w_ukv", "ev_g_idx_k", "ev_w_out",
        "ev_norm_ffn", "ev_w_gate", "ev_w_up", "ev_w_down", "od_norm_mix", "od_w_qkv", "od_lambda_q1", "od_lambda_k1",
        "od_lambda_q2", "od_lambda_k2", "od_g_sub", "od_w_out", "od_norm_ffn", "od_w_router", "od_w_gate_e", "od_w_up_e",
        "od_w_down_e", "final_norm"]


def _shape_constants():
    import numpy as np
    c = np.zeros((P, N_CONST), np.float32)
    c[:, K_ID:K_ID + P] = np.eye(P)
    c[:, K_IOTA:K_IOTA + P] = np.arange(P)
    c[:, K_TRI:K_TRI + P] = np.triu(np.ones((P, P)), 1)
    q, k = np.arange(S) // 64, np.arange(S) // 64
    hid = np.where(k[None, :] <= q[:, None], 0.0, NEG)
    c[:, K_HID:K_HID + P] = hid[0:P, 0:P]
    c[:, K_HID + P:K_HID + P + S] = hid[P:, :]
    c[:, K_E:K_E + 8] = np.arange(8)
    r = []
    for dim in (32, 16, 8):
        inv = np.float32(500000.0) ** (-np.arange(0, dim, 2, dtype=np.float32) / np.float32(dim))
        ang = (np.arange(S, dtype=np.float32)[:, None] * inv[None, :]).astype(np.float64)
        r += [np.cos(ang), np.sin(ang)]
    return c, np.concatenate(r, axis=1).astype(np.float32)


def kernel(**inputs):
    import numpy as _np
    import concourse.bacc as _bacc
    from concourse import mybir as _mybir
    from concourse.bass_utils import run_bass_kernel_spmd as _run

    nc = _bacc.Bacc("TRN2", target_bir_lowering=False, num_devices=1)
    arrays, aps = {}, {}
    consts, rope = _shape_constants()
    given = {name: _np.ascontiguousarray(inputs[name]) for name in _INS}
    for name, v in [*given.items(), ("consts", consts), ("rope", rope)]:
        arrays[f"in_{name}_dram"] = v
        aps[name] = nc.dram_tensor(f"in_{name}_dram", v.shape, _mybir.dt.from_np(v.dtype), kind="ExternalInput").ap()
    out = nc.dram_tensor("out_0_dram", (1, S, D), _mybir.dt.float32, kind="ExternalOutput").ap()
    trunk(nc, {**aps, "out": out})
    r = _run(nc, [arrays], core_ids=[0])
    return r.results[0]["out_0_dram"]
```
